# Optimizing a Trainium2 kernel written in Bass

```python
import math
import jax, jax.numpy as jnp
from jax import lax
import numpy as np

D_MODEL = 2048
BATCH = 1
SEQ = 256
DEPTH = 1

CHUNK = 64
HEAD_DIM = 128
SWA_Q_HEADS = 8
SWA_KV_HEADS = 2
WINDOW = 128
WINDOW_CHUNKS = WINDOW // CHUNK
SB_HEADS = 8
SB_BLOCK = 128
DN_HEADS = 8
DN_CONV = 4
SWA_Q_W = SWA_Q_HEADS * HEAD_DIM
SWA_KV_W = SWA_KV_HEADS * HEAD_DIM
SB_W = SB_HEADS * HEAD_DIM
DN_W = DN_HEADS * HEAD_DIM
IN_WIDTHS = (SWA_Q_W, SWA_KV_W, SWA_KV_W,
             SB_W, SB_W, SB_W,
             3 * DN_W, DN_HEADS, DN_HEADS, DN_W,
             D_MODEL, D_MODEL, D_MODEL)
N_IN = sum(IN_WIDTHS)
N_GROUPS = 4
EXPERTS_PER_GROUP = 8
N_EXPERTS = N_GROUPS * EXPERTS_PER_GROUP
TOP_K = 2
D_EXPERT = 512
MOE_BLOCK = 128
PLE_DIM = 256

kernel_name = "hybrid_swa_stickbreak_gdn_hiermoe"

def rms_norm(x, gain, eps=1e-6):
    xf = x.astype(jnp.float32)
    y = xf * lax.rsqrt(jnp.mean(xf * xf, axis=-1, keepdims=True) + eps)
    return (y * gain.astype(jnp.float32)).astype(x.dtype)

def l2_norm(x, eps=1e-6):
    return x * lax.rsqrt(jnp.sum(x * x, axis=-1, keepdims=True) + eps)

def sliding_window_sink_attention(q, k, v, q_gain, k_gain, sinks):
    B, S, Hq, d = q.shape
    Hkv = k.shape[2]
    G = Hq // Hkv
    nC = S // CHUNK
    q = rms_norm(q, q_gain).astype(jnp.float32)
    k = rms_norm(k, k_gain).astype(jnp.float32)
    v = v.astype(jnp.float32)
    qc = q.reshape(B, nC, CHUNK, Hkv, G, d)
    kc = k.reshape(B, nC, CHUNK, Hkv, d)
    vc = v.reshape(B, nC, CHUNK, Hkv, d)

    def band(t):
        parts = [jnp.pad(t, ((0, 0), (j, 0), (0, 0), (0, 0), (0, 0)))[:, :nC]
                 for j in range(WINDOW_CHUNKS - 1, -1, -1)]
        return jnp.concatenate(parts, axis=2)

    kb, vb = band(kc), band(vc)
    offs = jnp.repeat(jnp.arange(WINDOW_CHUNKS - 1, -1, -1), CHUNK)
    valid = (jnp.arange(nC)[:, None] - offs[None, :]) >= 0
    scores = jnp.einsum('bcqhgd,bckhd->bchgqk', qc, kb) * (d ** -0.5)
    scores = jnp.where(valid[None, :, None, None, None, :], scores, -jnp.inf)
    sink = sinks.astype(jnp.float32).reshape(Hkv, G)[None, None, :, :, None, None]
    m = jnp.maximum(jnp.max(scores, axis=-1, keepdims=True), sink)
    e = jnp.exp(scores - m)
    probs = e / (jnp.sum(e, axis=-1, keepdims=True) + jnp.exp(sink - m))
    out = jnp.einsum('bchgqk,bckhd->bcqhgd', probs, vb)
    return out.reshape(B, S, Hq * d)

def stick_breaking_attention(q, k, v, q_gain, k_gain):
    B, S, H, d = q.shape
    q = rms_norm(q, q_gain).astype(jnp.float32) * (d ** -0.5)
    k = rms_norm(k, k_gain).astype(jnp.float32)
    v = v.astype(jnp.float32)
    outs = []
    for start in range(0, S, SB_BLOCK):
        end = start + SB_BLOCK
        z = jnp.einsum('bqhd,bkhd->bhqk', q[:, start:end], k[:, :end])
        causal = jnp.arange(end)[None, :] < (start + jnp.arange(SB_BLOCK))[:, None]
        log_not = jnp.where(causal, jax.nn.log_sigmoid(-z), 0.0)
        between = lax.cumsum(log_not, axis=3, reverse=True) - log_not
        a = jnp.where(causal, jnp.exp(jax.nn.log_sigmoid(z) + between), 0.0)
        outs.append(jnp.einsum('bhqk,bkhd->bqhd', a, v[:, :end]))
    return jnp.concatenate(outs, axis=1).reshape(B, S, H * d)

def causal_depthwise_conv(x, w):
    K = w.shape[0]
    S = x.shape[1]
    xp = jnp.pad(x, ((0, 0), (K - 1, 0), (0, 0)))
    y = xp[:, 0:S] * w[0]
    for j in range(1, K):
        y = y + xp[:, j:j + S] * w[j]
    return y

def gated_delta_net(q, k, v, a, b, z, a_log, dt_bias, out_gain):
    B, S, H, d = q.shape
    nC = S // CHUNK
    f32 = jnp.float32
    q = l2_norm(q.astype(f32)) * (d ** -0.5)
    k = l2_norm(k.astype(f32))
    v = v.astype(f32)
    beta = jax.nn.sigmoid(b.astype(f32))
    g = -jnp.exp(a_log.astype(f32)) * jax.nn.softplus(a.astype(f32) + dt_bias.astype(f32))

    def chunks(t):
        return t.reshape(B, nC, CHUNK, H, -1).transpose(0, 3, 1, 2, 4)

    qc, kc, vc = chunks(q), chunks(k), chunks(v)
    bc = chunks(beta[..., None])[..., 0]
    gc = lax.cumsum(chunks(g[..., None])[..., 0], axis=3)
    idx = jnp.arange(CHUNK)
    lower_incl = idx[:, None] >= idx[None, :]
    strict = idx[:, None] > idx[None, :]
    decay = jnp.exp(jnp.where(lower_incl, gc[..., :, None] - gc[..., None, :], -jnp.inf))
    kbeta = kc * bc[..., None]
    n_mat = -jnp.where(strict, jnp.einsum('bhncd,bhnkd->bhnck', kbeta, kc) * decay, 0.0)
    t_mat = jnp.eye(CHUNK, dtype=f32) + n_mat
    power = n_mat
    for _ in range(int(math.log2(CHUNK)) - 1):
        power = power @ power
        t_mat = t_mat + t_mat @ power
    u = t_mat @ (vc * bc[..., None])
    w = t_mat @ (kbeta * jnp.exp(gc)[..., None])
    attn_qk = jnp.where(lower_incl, jnp.einsum('bhncd,bhnkd->bhnck', qc, kc) * decay, 0.0)
    g_last = gc[..., -1]

    def step(state, xs):
        q_i, k_i, u_i, w_i, a_i, g_i, gl_i = xs
        v_new = u_i - w_i @ state
        o = (q_i * jnp.exp(g_i)[..., None]) @ state + a_i @ v_new
        state = (state * jnp.exp(gl_i)[..., None, None]
                 + jnp.einsum('bhck,bhcv->bhkv', k_i * jnp.exp(gl_i[..., None] - g_i)[..., None], v_new))
        return state, o

    xs = tuple(jnp.moveaxis(t, 2, 0) for t in (qc, kc, u, w, attn_qk, gc, g_last))
    state0 = jnp.zeros((B, H, d, d), f32)
    _, o = lax.scan(step, state0, xs)
    o = o.transpose(1, 0, 3, 2, 4).reshape(B, S, H, d)
    o = rms_norm(o, out_gain) * jax.nn.silu(z.astype(f32).reshape(B, S, H, d))
    return o.reshape(B, S, H * d)

def hierarchical_moe(h, w_group, b_group, w_router, b_router, w_gate, w_up, w_down):
    B, S, D = h.shape
    N = B * S
    hf = h.reshape(N, D)
    group_logits = (hf @ w_group).astype(jnp.float32) + b_group.astype(jnp.float32)
    group_probs = jax.nn.softmax(group_logits, axis=-1)
    group_idx = jnp.argmax(group_logits, axis=-1)
    group_p = jnp.take_along_axis(group_probs, group_idx[:, None], axis=1)[:, 0]
    exp_logits = ((hf @ w_router).astype(jnp.float32) + b_router.astype(jnp.float32)).reshape(
        N, N_GROUPS, EXPERTS_PER_GROUP)
    in_group = jnp.take_along_axis(exp_logits, group_idx[:, None, None], axis=1)[:, 0]
    top_vals, top_idx = lax.top_k(in_group, TOP_K)
    weights = jax.nn.softmax(top_vals, axis=-1) * group_p[:, None]
    expert_id = group_idx[:, None] * EXPERTS_PER_GROUP + top_idx

    M = N * TOP_K
    flat_e = expert_id.reshape(M)
    order = jnp.argsort(flat_e)
    sorted_e = flat_e[order]
    sorted_tok = order // TOP_K
    counts = jnp.bincount(flat_e, length=N_EXPERTS)
    padded = (counts + MOE_BLOCK - 1) // MOE_BLOCK * MOE_BLOCK
    pad_end = jnp.cumsum(padded)
    pad_start = pad_end - padded
    start = jnp.cumsum(counts) - counts
    dest = pad_start[sorted_e] + jnp.arange(M) - start[sorted_e]
    n_blocks = (M + N_EXPERTS * (MOE_BLOCK - 1) + MOE_BLOCK - 1) // MOE_BLOCK
    P = n_blocks * MOE_BLOCK
    buf_tok = jnp.zeros((P,), jnp.int32).at[dest].set(sorted_tok.astype(jnp.int32))
    x_buf = hf[buf_tok].reshape(n_blocks, MOE_BLOCK, D)
    block_e = jnp.minimum(jnp.searchsorted(pad_end, jnp.arange(n_blocks) * MOE_BLOCK, side='right'),
                          N_EXPERTS - 1)

    def expert_block(args):
        xb, e = args
        hid = jax.nn.silu(xb @ w_gate[e]) * (xb @ w_up[e])
        return hid @ w_down[e]

    y_buf = lax.map(expert_block, (x_buf, block_e)).reshape(P, D)
    y_sorted = y_buf[dest]
    w_sorted = weights.reshape(M)[order].astype(y_sorted.dtype)
    y = jax.ops.segment_sum(y_sorted * w_sorted[:, None], sorted_tok, num_segments=N)
    return y.reshape(B, S, D)

def setup_inputs(seed: int = 0) -> dict:
    key = jax.random.key(seed)
    ks = jax.random.split(key, 32)
    f32 = jnp.float32

    def normal(i, shape, fan_in):
        return jax.random.normal(ks[i], shape, f32) * (fan_in ** -0.5)

    def gain(i, shape):
        return 1.0 + 0.02 * jax.random.normal(ks[i], shape, f32)

    L = DEPTH
    return {
        "x": jax.random.normal(ks[0], (BATCH, SEQ, D_MODEL), f32),
        "p": jax.random.normal(ks[1], (DEPTH, BATCH, SEQ, PLE_DIM), f32),
        "mix_norm": gain(2, (L, D_MODEL)),
        "w_in": normal(3, (L, D_MODEL, N_IN), D_MODEL),
        "swa_q_norm": gain(4, (L, HEAD_DIM)),
        "swa_k_norm": gain(5, (L, HEAD_DIM)),
        "swa_sinks": 0.5 * jax.random.normal(ks[6], (L, SWA_Q_HEADS), f32),
        "sb_q_norm": gain(7, (L, HEAD_DIM)),
        "sb_k_norm": gain(8, (L, HEAD_DIM)),
        "dn_conv": normal(9, (L, DN_CONV, 3 * DN_W), DN_CONV),
        "dn_a_log": jnp.log(jax.random.uniform(ks[10], (L, DN_HEADS), f32, 1.0, 8.0)),
        "dn_dt_bias": 0.1 * jax.random.normal(ks[11], (L, DN_HEADS), f32),
        "dn_out_norm": gain(12, (L, HEAD_DIM)),
        "w_branch_a": normal(13, (L, SWA_Q_W, D_MODEL), SWA_Q_W),
        "w_branch_b": normal(14, (L, SB_W, D_MODEL), SB_W),
        "w_branch_c": normal(15, (L, DN_W, D_MODEL), DN_W),
        "w_out": normal(16, (L, D_MODEL, D_MODEL), D_MODEL),
        "ffn_norm": gain(17, (L, D_MODEL)),
        "w_group": normal(18, (L, D_MODEL, N_GROUPS), D_MODEL),
        "b_group": 0.01 * jax.random.normal(ks[19], (L, N_GROUPS), f32),
        "w_router": normal(20, (L, D_MODEL, N_EXPERTS), D_MODEL),
        "b_router": 0.01 * jax.random.normal(ks[21], (L, N_EXPERTS), f32),
        "w_e_gate": normal(22, (L, N_EXPERTS, D_MODEL, D_EXPERT), D_MODEL),
        "w_e_up": normal(23, (L, N_EXPERTS, D_MODEL, D_EXPERT), D_MODEL),
        "w_e_down": normal(24, (L, N_EXPERTS, D_EXPERT, D_MODEL), D_EXPERT),
        "ple_norm": gain(25, (L, D_MODEL)),
        "w_ple_gate": normal(26, (L, D_MODEL, D_MODEL), D_MODEL),
        "w_ple_proj": normal(27, (L, PLE_DIM, D_MODEL), PLE_DIM),
    }

def reference(x, p, mix_norm, w_in, swa_q_norm, swa_k_norm, swa_sinks, sb_q_norm, sb_k_norm,
              dn_conv, dn_a_log, dn_dt_bias, dn_out_norm, w_branch_a, w_branch_b, w_branch_c,
              w_out, ffn_norm, w_group, b_group, w_router, b_router, w_e_gate, w_e_up, w_e_down,
              ple_norm, w_ple_gate, w_ple_proj):
    B, S, _ = x.shape
    split_at = [int(c) for c in np.cumsum(IN_WIDTHS)[:-1]]
    for i in range(DEPTH):
        xn = rms_norm(x, mix_norm[i])
        proj = xn @ w_in[i]
        (aq, ak, av, bq, bk, bv, c_qkv, c_a, c_b, c_z, g_a, g_b, g_c) = jnp.split(proj, split_at, axis=-1)

        out_a = sliding_window_sink_attention(
            aq.reshape(B, S, SWA_Q_HEADS, HEAD_DIM), ak.reshape(B, S, SWA_KV_HEADS, HEAD_DIM),
            av.reshape(B, S, SWA_KV_HEADS, HEAD_DIM), swa_q_norm[i], swa_k_norm[i], swa_sinks[i])
        out_b = stick_breaking_attention(
            bq.reshape(B, S, SB_HEADS, HEAD_DIM), bk.reshape(B, S, SB_HEADS, HEAD_DIM),
            bv.reshape(B, S, SB_HEADS, HEAD_DIM), sb_q_norm[i], sb_k_norm[i])
        c_qkv = jax.nn.silu(causal_depthwise_conv(c_qkv, dn_conv[i]))
        cq, ck, cv = jnp.split(c_qkv, 3, axis=-1)
        out_c = gated_delta_net(
            cq.reshape(B, S, DN_HEADS, HEAD_DIM), ck.reshape(B, S, DN_HEADS, HEAD_DIM),
            cv.reshape(B, S, DN_HEADS, HEAD_DIM), c_a, c_b, c_z, dn_a_log[i], dn_dt_bias[i], dn_out_norm[i])

        merged = (jax.nn.sigmoid(g_a) * (out_a.astype(xn.dtype) @ w_branch_a[i])
                  + jax.nn.sigmoid(g_b) * (out_b.astype(xn.dtype) @ w_branch_b[i])
                  + jax.nn.sigmoid(g_c) * (out_c.astype(xn.dtype) @ w_branch_c[i]))
        x = x + merged @ w_out[i]

        x = x + hierarchical_moe(rms_norm(x, ffn_norm[i]), w_group[i], b_group[i], w_router[i],
                                 b_router[i], w_e_gate[i], w_e_up[i], w_e_down[i])

        ple_gate = jax.nn.sigmoid(rms_norm(x, ple_norm[i]) @ w_ple_gate[i])
        x = x + ple_gate * (p[i] @ w_ple_proj[i])
    return x


_drawn_inputs = setup_inputs


def setup_inputs(seed=0):
    import zlib

    import numpy as np

    out = dict(_drawn_inputs(seed))
    spreads = {}
    factors = {'swa_q_norm': 6.576,
     'swa_k_norm': 5.509,
     'swa_sinks': 8.0,
     'sb_q_norm': 19.036,
     'sb_k_norm': 10.722,
     'dn_dt_bias': 3.016,
     'dn_out_norm': 4.706,
     'b_group': 5.133,
     'b_router': 16.931,
     'ple_norm': 58.367,
     'ffn_norm': 2.801}
    for name, (base, spread) in spreads.items():
        noise = np.random.default_rng([zlib.crc32(name.encode()), seed]).standard_normal(out[name].shape)
        drawn = base * np.exp(spread * noise) if base else spread * noise
        out[name] = __import__('jax').numpy.asarray(drawn.astype(out[name].dtype))
    for name, factor in factors.items():
        out[name] = (out[name] * factor).astype(out[name].dtype)
    return out
```

```python
import concourse.bass as bass
from concourse import mybir
from contextlib import ExitStack

F32 = mybir.dt.float32
F32R = mybir.dt.float32r
I32 = mybir.dt.int32
ALU = mybir.AluOpType
ACT = mybir.ActivationFunctionType
AX = mybir.AxisListType
ds = bass.ds

P = 128
D = 2048
KT = D // P
S = 256
TT = S // P
CH = 64
NCH = S // CH
NH = 8
SWQ, SWK, SWV = 0, 1024, 1280
SBQ, SBK, SBV = 1536, 2560, 3584
DNQ, DNK, DNV, DNAB, DNZ = 4608, 5632, 6656, 7680, 7696
GATE = 8720
N_IN = GATE + 3 * D
NE, NG, EPG = 32, 4, 8
DE = 512
WIN = 32
NSLOT = 2 * S
PLE = 256
HS = P ** -0.5
EPS = 1e-6
BIG = 1e30

F_NGC, F_BETA, F_BEG, F_KD, F_SINK, F_EGL, F_CONV = 0, 2, 4, 6, 8, 9, 13
NF = 25
EXP_LN_SET = 6
PAIRS, PRO = 4, 4


def hybrid_trunk(nc, x, p, mix_norm, w_in, swa_q_norm, swa_k_norm, swa_sinks, sb_q_norm, sb_k_norm, dn_conv,
                 dn_a_log, dn_dt_bias, dn_out_norm, w_branch_a, w_branch_b, w_branch_c, w_out, ffn_norm, w_group,
                 b_group, w_router, b_router, w_e_gate, w_e_up, w_e_down, ple_norm, w_ple_gate, w_ple_proj, out):
    ctx = ExitStack()
    with ctx:
        def sb(name, shape, dt=F32):
            return ctx.enter_context(nc.sbuf_tensor(name, shape, dt))

        sems = {}

        base = {name: (group, i) for group, names in (
            ("pool_step", ("iota", "ident", "consts")),
            ("pe_step", ("rows_bc", "abT", "ab_tok", "ksw_ss", "vT", "gc", "logits", "counts", "slots", "pT_mm")),
            ("act_step", ("x_rms", "abT_sb", "ksw_sq", "ksw_rt", "v_raw", "vt_sw", "ab_sp", "gc_exp", "egl", "x1_rms", "gexps",
                          "x3_rms")),
            ("dve_step", ("eps", "rb", "kT_sw", "ab_v", "g", "gc_sb", "maxes", "chosen", "windows", "jobs", "sel",
                          "x2_all", "pT"))) for i, name in enumerate(names)}
        base.update(h_tok=("x_n", 2), x3n=("x_n", 4), hT=("xnT", 8), hT_in=("xnT_in", 8), x3T=("xnT", 16),
                    x3T_in=("xnT_in", 16))
        for b in range(3):
            base[f"gfull{b}"] = (f"full{b}", 16 * (1 + 2 * NH))
            base[f"plfull{b}"] = (f"mfull{b}", 16 * NE)
        base["g_hi"], base["g_lo"] = ("w_hi", PRO + 8 * NH), ("w_lo", PRO + 8 * NH)
        base["wofull2"], base["wofull3"] = ("full0", 16 * (1 + 2 * NH + KT)), ("wofull0", 16)

        def sem(name):
            name = base.get(name, (name, 0))[0]
            if name not in sems:
                sems[name] = ctx.enter_context(nc.semaphore(name))
            return sems[name]

        def event(name, n):
            name, before = base.get(name, (name, 0))
            return sem(name), n + before

        ring_at = -(-nc.sbuf_base // 32) * 32
        ring = sb("ring", [P, 24576])
        x_tok_at = -(-nc.sbuf_base // 32) * 32
        x_tok = sb("x_tok", [P, TT, D])
        xnT_at = -(-nc.sbuf_base // 32) * 32
        xnT = sb("xnT", [P, KT, S])
        mo_at = -(-nc.sbuf_base // 32) * 32
        mo = sb("mo", [P, 10240])
        hp_at = -(-nc.sbuf_base // 32) * 32
        hp = sb("hp", [P, 4096])
        merged = mo[:, 0:4096].rearrange("p (f s) -> p f s", f=KT)
        outs = mo[:, 4096:10240].rearrange("p (b h s) -> p b h s", b=3, h=NH)
        xs = mo[:, 0:KT * (NSLOT + WIN)].rearrange("p (t s) -> p t s", t=KT)
        Gb = hp[:, 0:2048].rearrange("p (h s) -> p h s", h=NH)
        nBb = hp[:, 2048:4096].rearrange("p (h s) -> p h s", h=NH)

        slot = [ring[:, 2048 * s:2048 * s + 2048].rearrange("p (t n) -> p t n", t=KT) for s in range(8)]
        arenas = [[ring, 16384, 24576], [mo, 0, 4096]]

        def tmp(n):
            for a in arenas:
                if a[1] + n <= a[2]:
                    a[1] += n
                    return a[0][:, a[1] - n:a[1]]
            raise MemoryError(n)

        cv, ex = tmp(768), tmp(768)
        sq_sb, r_sb, qk_sb, sq_dn, r_dn, qk_dn, vt_sw, pttt = (tmp(512) for _ in range(8))
        za, sp, am, smx, pT = (tmp(384) for _ in range(5))
        sq_sw, r_sw, q_sw, ez, pm, v_sw, decT, eG = (tmp(256) for _ in range(8))
        attnT, kbg, vb, kdec, nwT, vn, raw_z, raw_sw, raw_v, v_sb = (tmp(256) for _ in range(10))
        state = tmp(P)
        abw, abT = r_dn[:, 0:S], r_dn[:, S:2 * S]
        abw = abw.rearrange("p (t n) -> p t n", t=KT)
        v_sb = v_sb.rearrange("p (t n) -> p t n", t=TT)
        vt_sw = vt_sw.rearrange("p (g n) -> p g n", g=2)
        raw_sb = sb("raw_sb", [P, 2, S])
        raw_dn = sb("raw_dn", [P, 3, 3 + S])
        kT_sw = sb("kT_sw", [P, 2, S])
        hs = sb("hs", [P, F_CONV])
        hc = sb("hc", [P, NF - F_CONV])
        sm = sb("sm", [P, 16])
        head = sb("head", [P, NF, NH])
        gt = q_sw[:, 0:128].rearrange("p (i n) -> p i n", i=8)
        rows = sb("rows", [1, 64])
        rb = sb("rb", [P, 64])
        gains = sb("gains", [P, 8])
        ng, ngf, ngp = sb("ng", [P, KT]), sb("ngf", [P, KT]), sb("ngp", [P, KT])
        rs2 = sb("rs2", [P, 8])
        convw = sb("convw", [P, 24, 4])
        epsb = sb("epsb", [P, 1])
        ident, ones, nones, negL, upper, capdn, nmask, cumc, sufc = (
            sb(n, [P, P]) for n in ("ident", "ones", "nones", "negL", "upper", "capdn", "nmask", "cumc", "sufc"))
        capsb, masksw = sb("capsb", [P, 3, P]), sb("masksw", [P, 3, P])
        iota = sb("iota", [P, NSLOT + WIN])
        ioi = xnT[:, :, :].rearrange("p t s -> p (t s)")[:, 0:NSLOT + WIN].bitcast(I32)
        wr = sb("wr", [P, KT, NG + NE])
        lg = sb("lg", [P, TT, NG + NE])
        desc = sb("desc", [P, NG + NE])
        rt = raw_dn[:, :, :].rearrange("p a b -> p (a b)")[:, 0:768].rearrange("p (i t e) -> p i t e", i=12, t=TT)
        rsm = sb("rsm", [P, 16, TT])
        thr = sb("thr", [NE, 8])
        cntb, nwb = raw_sb[0:NE, 0, 0:P], raw_sb[0:NE, 0, P:S]
        cmp8 = sb("cmp8", [NE, 8])
        posw = sb("posw", [P, 4, NE])
        jobs = sb("jobs", [1, 3, NE], I32)
        pw = sb("pw", [P, 4])
        tail = mo[:, KT * (NSLOT + WIN):10240]
        xw = tail[:, 0:512].rearrange("p (t s) -> p t s", t=KT)
        sw = tail[:, 512:768].rearrange("p (t s) -> p t s", t=TT)
        swT = tail[:, 768:1024].rearrange("p (t s) -> p t s", t=TT)
        hh, hT, eg = tail[:, 1024:1152], tail[:, 1152:1280], tail[:, 1280:1408]
        ysb = raw_dn[:, :, :].rearrange("p a b -> p (a b)")[:, 0:512]
        pple = xnT[:, :, :].rearrange("p t s -> p (t s)").rearrange("p (t n) -> p t n", t=TT)
        h_tok = hp[:, :].rearrange("p (t k c) -> p t k c", t=TT, k=KT)
        x_n = hp[:, :].rearrange("p (t n) -> p t n", t=TT)
        x3T = hp[:, :].rearrange("p (t s) -> p t s", t=KT)
        x3n = mo[:, 0:4096].rearrange("p (t n) -> p t n", t=TT)
        dump = mo[:, 4096:6144]
        br_slot = [hp[:, 1024 * b:1024 * b + 1024].rearrange("p (t n) -> p t n", t=8) for b in range(3)]
        xh = nc.alloc_sbuf_tensor_at("xh", [P, KT, S], F32R, offset=x_tok_at)
        xl = nc.alloc_sbuf_tensor_at("xl", [P, KT, S], F32R, offset=xnT_at)
        wh = [nc.alloc_sbuf_tensor_at(f"wh{p}", [P, KT, P], F32R, offset=ring_at + 8192 * (PAIRS + p)) for p in range(PAIRS)]
        wl = [nc.alloc_sbuf_tensor_at(f"wl{p}", [P, KT, P], F32R, offset=ring_at + 8192 * p) for p in range(PAIRS)]
        h_hi = nc.alloc_sbuf_tensor_at("h_hi", [P, TT, KT, P], F32R, offset=xnT_at)
        h_lo = nc.alloc_sbuf_tensor_at("h_lo", [P, TT, KT, P], F32R, offset=hp_at)
        sel = nc.alloc_sbuf_tensor_at("sel", [P, TT, NSLOT], F32R, offset=mo_at + 4 * KT * (NSLOT + WIN))
        abh, abl = (nc.alloc_sbuf_tensor_at(n, [P, KT, 16], F32R, offset=mo_at + 4 * o) for n, o in (("abh", 8192), ("abl", 8448)))
        wo_slot = [ring[:, c:c + 8192].rearrange("p (t n) -> p t n", t=KT) for c in (16384, 8192, 0, 16384)]
        m_flat = [ring[:, 4096 * i:4096 * i + 4096].rearrange("p (a n) -> p a n", a=1) for i in range(6)]
        m_gu = [ring[:, 4096 * i:4096 * i + 4096].rearrange("p (t n) -> p t n", t=8) for i in range(4)]
        m_down = [ring[:, 4096 * i:4096 * i + 4096].rearrange("p (a t n) -> p a t n", a=1, t=2) for i in (4, 5)]
        pl_slot = [ring[:, 8192 * i:8192 * i + 8192].rearrange("p (t n) -> p t n", t=KT) for i in range(3)]
        esig = [ring[:, 14336 + 256 * b:14592 + 256 * b] for b in range(3)]
        macc = ring[:, 15104:15360]
        pe_e = [mo[:, 8192 + 512 * i:8704 + 512 * i] for i in range(2)]
        wpp = hp[:, :].rearrange("p (t n) -> p t n", t=2)
        pin = raw_sb

        bank = [ctx.enter_context(nc.psum_tensor(f"bank{i}", [P, 512], F32)) for i in range(8)]

        ab_psum = bank[6][:, 64:96].rearrange("p (t n) -> p t n", t=TT)

        w_in_v = w_in.rearrange("a (t p) n -> p (a t) n", p=P)
        w_br_v = [w.rearrange("a (t p) n -> p (a t) n", p=P) for w in (w_branch_a, w_branch_b, w_branch_c)]
        w_out_v = w_out.rearrange("a (t p) n -> p (a t) n", p=P)
        weg_v = w_e_gate.rearrange("a e (p t) n -> p (a e) (t n)", p=P)
        weu_v = w_e_up.rearrange("a e (p t) n -> p (a e) (t n)", p=P)
        wed_v = w_e_down.rearrange("a e (t p) n -> p (a e) t n", p=P)
        wpg_v = w_ple_gate.rearrange("a (t p) n -> p (a t) n", p=P)
        wpp_v = w_ple_proj.rearrange("a (t p) n -> p (a t) n", p=P)
        out_v = out.rearrange("a (t p) n -> p (a t) n", p=P)

        def tile_cols(s, h):
            return (DNQ, DNK, DNV, SBV, SBQ, SBK, DNZ, SWQ)[s] + h * P

        ctx.enter_context(nc.allow_non_contiguous_dma(reason="small parameters by partition"))
        block = ctx.enter_context(nc.Block())

        @block.sync
        def _(sp):
            sp.dma_start(x_tok[:], x.rearrange("a (t p) n -> p (a t) n", p=P)).then_inc(sem("x_in"), 16)
            small = [(ng[:], mix_norm.rearrange("a (t p) -> p (a t)", p=P)),
                     (abw[:], w_in_v[:, :, DNAB:DNAB + 16]),
                     (rows[0:1, 0:8], dn_dt_bias), (rows[0:1, 8:16], dn_a_log), (rows[0:1, 16:24], swa_sinks),
                     (rows[0:1, 24:28], b_group), (rows[0:1, 28:60], b_router),
                     (gains[:, 0:1], swa_q_norm.rearrange("a p -> p a")),
                     (gains[:, 1:2], swa_k_norm.rearrange("a p -> p a")),
                     (gains[:, 2:3], sb_q_norm.rearrange("a p -> p a")),
                     (gains[:, 3:4], sb_k_norm.rearrange("a p -> p a")),
                     (gains[:, 4:5], dn_out_norm.rearrange("a p -> p a")),
                     (ngf[:], ffn_norm.rearrange("a (p t) -> p (a t)", p=P)),
                     (ngp[:], ple_norm.rearrange("a (t p) -> p (a t)", p=P)),
                     (wr[:, :, 0:4], w_group.rearrange("a (p t) n -> p (a t) n", p=P)),
                     (wr[:, :, 4:36], w_router.rearrange("a (p t) n -> p (a t) n", p=P))]
            small += [(convw[:, :, j:j + 1], dn_conv[:, j, :].rearrange("a (c p) -> p c a", p=P)) for j in range(4)]
            for i, (to, of) in enumerate(small):
                sp.dma_start(to, of).then_inc(sem("small_in"), 16)
            assert len(small) == 20
            for s, c in enumerate((SWK, SWK + P, SWV, SWV + P)):
                sp.dma_start(slot[s], w_in_v[:, :, c:c + P]).then_inc(sem(f"full{s}"), 16)
            for s in range(8):
                sp.wait_ge(*event("tile_mm", s + 1))
                sp.dma_start(slot[s % PAIRS], w_in_v[:, :, ds(tile_cols(s, 0), P)]).then_inc(sem(f"full{s % PAIRS}"), 16)
            with sp.Fori(1, NH) as h:
                for s in range(8):
                    sp.wait_ge(*event("tile_mm", 8 * h + s + 1))
                    sp.dma_start(slot[s % PAIRS], w_in_v[:, :, ds(tile_cols(s, 1) + (h - 1) * P, P)])\
                        .then_inc(sem(f"full{s % PAIRS}"), 16)
            for b in range(3):
                sp.wait_ge(*event("tile_mm", 8 * NH + b + 1))
                sp.dma_start(slot[b], w_in_v[:, :, GATE + b * D:GATE + b * D + P]).then_inc(sem(f"gfull{b}"), 16)
            sp.wait_ge(*event("decays_used", NH))
            for b in range(3):
                sp.dma_start(br_slot[b], w_br_v[b][:, :, 0:P]).then_inc(sem(f"bfull{b}"), 16)
            sp.wait_ge(*event("head", NH + 1))
            sp.dma_start(wo_slot[0], w_out_v[:, :, 0:512]).then_inc(sem("wofull0"), 16)
            with sp.Fori(1, KT) as f:
                for b in range(3):
                    sp.wait_ge(*event(f"gused{b}", f))
                    sp.dma_start(slot[b], w_in_v[:, :, ds(GATE + b * D + f * P, P)]).then_inc(sem(f"gfull{b}"), 16)
                    sp.wait_ge(*event(f"bused{b}", f))
                    sp.dma_start(br_slot[b], w_br_v[b][:, :, ds(P + (f - 1) * P, P)]).then_inc(sem(f"bfull{b}"), 16)
            def expert_piece(i, e):
                if i < 2:
                    return sp.dma_start(m_flat[i], weg_v[:, ds(e, 1), i * 4096:i * 4096 + 4096])
                if i < 4:
                    return sp.dma_start(m_flat[i], weu_v[:, ds(e, 1), (i - 2) * 4096:(i - 2) * 4096 + 4096])
                return sp.dma_start(m_down[i - 4], wed_v[:, ds(e, 1), 2 * (i - 4):2 * (i - 4) + 2, :])

            for b in range(3):
                sp.wait_ge(*event(f"gused{b}", KT))
            sp.wait_ge(*event("merged", KT))
            sp.dma_start(wo_slot[1], w_out_v[:, :, 512:1024]).then_inc(sem("wofull1"), 16)
            sp.dma_start(x_tok[:], x.rearrange("a (t p) n -> p (a t) n", p=P)).then_inc(sem("x_in"), 16)
            sp.dma_start(wo_slot[2], w_out_v[:, :, 1024:1536]).then_inc(sem("wofull2"), 16)
            sp.wait_ge(*event("wo_mm", 2))
            sp.dma_start(wo_slot[3], w_out_v[:, :, 1536:2048]).then_inc(sem("wofull3"), 16)
            for i in (2, 3, 0, 1, 4, 5):
                sp.wait_ge(*event("wo_mm", (6, 4, 8)[i // 2]))
                expert_piece(i, 0).then_inc(sem(f"mfull{i}"), 16)
            sp.wait_ge(*event("gathered", KT))
            for j in range(TT):
                sp.dma_start(pin[:, j, :], p.rearrange("l a (t p) n -> p (l a t) n", p=P)[:, j, :]).then_inc(sem("p_in"), 16)
            sp.dma_start(wpp[:], wpp_v).then_inc(sem("p_in"), 16)
            with sp.Fori(1, NE) as e:
                for i in range(6):
                    sp.wait_ge(*event(f"mused{i}", e))
                    expert_piece(i, e).then_inc(sem(f"mfull{i}"), 16)
            for n in range(4):
                s = n % 3
                if n < 3:
                    sp.wait_ge(*event(f"mused{2 * s}", NE))
                    sp.wait_ge(*event(f"mused{2 * s + 1}", NE))
                else:
                    sp.wait_ge(*event("gple_done", 2))
                sp.dma_start(pl_slot[s], wpg_v[:, :, n * 512:n * 512 + 512]).then_inc(sem(f"plfull{s}"), 16)
            for n in range(4):
                for t in range(TT):
                    sp.wait_ge(*event("result", 2 * n + t + 1))
                    sp.dma_start(out_v[:, t, n * 512:n * 512 + 512], x_tok[:, t, n * 512:n * 512 + 512])\
                      .then_inc(sem("stored"), 16)
            sp.wait_ge(*event("stored", 16 * 4 * TT))

        @block.gpsimd
        def _(pool):
            sel_ = pool.affine_select
            pool.iota(ioi, pattern=[[1, NSLOT + WIN]], base=0, channel_multiplier=0)
            pool.memset(ident[:], 0.0)
            pool.memset(ones[:], 1.0)
            pool.memset(nones[:], -1.0)
            pool.memset(capsb[:], 0.0)
            pool.memset(capdn[:], 0.0)
            pool.memset(masksw[:], 0.0)
            pool.drain()
            pool.tensor_copy(iota[:], ioi).then_inc(sem("iota"), 1)
            sel_(out=ident[:], in_=ident[:], compare_op=ALU.not_equal, fill=1.0, base=0, pattern=[[-1, P]],
                 channel_multiplier=1).then_inc(sem("ident"), 1)
            sel_(out=negL[:], in_=nones[:], compare_op=ALU.is_ge, fill=0.0, base=0, pattern=[[-1, P]], channel_multiplier=1)
            sel_(out=upper[:], in_=ones[:], compare_op=ALU.is_gt, fill=0.0, base=0, pattern=[[1, P]], channel_multiplier=-1)
            for b in (0, 2):
                sel_(out=capsb[:, b, :], in_=capsb[:, b, :], compare_op=ALU.is_gt, fill=-BIG, base=0,
                     pattern=[[1, P]], channel_multiplier=-1)
            sel_(out=capdn[:], in_=capdn[:], compare_op=ALU.is_ge, fill=-BIG, base=0, pattern=[[1, P]], channel_multiplier=-1)
            sel_(out=nmask[:], in_=nones[:], compare_op=ALU.is_gt, fill=0.0, base=0, pattern=[[1, P]], channel_multiplier=-1)
            sel_(out=cumc[:], in_=ones[:], compare_op=ALU.is_ge, fill=0.0, base=0, pattern=[[1, P]], channel_multiplier=-1)
            sel_(out=sufc[:], in_=ones[:], compare_op=ALU.is_gt, fill=0.0, base=0, pattern=[[-1, P]], channel_multiplier=1)
            pool.drain()
            pool.memset(capdn[0:CH, CH:P], -BIG)
            pool.memset(nmask[0:CH, CH:P], 0.0)
            pool.memset(cumc[0:CH, CH:P], 0.0)
            pool.drain()
            pool.memset(sufc[CH:P, 0:CH], 0.0)
            pool.memset(masksw[CH:P, 1, CH:P], -BIG)
            pool.drain()
            pool.memset(masksw[0:CH, 0, CH:P], -BIG)
            pool.memset(masksw[0:CH, 2, CH:P], -BIG)
            pool.drain()
            pool.memset(masksw[:, 1, 0:CH], -BIG)
            pool.tensor_scalar(desc[:, 0:NG], iota[:, 0:NG], -1.0, float(NG), ALU.mult, ALU.add)
            pool.tensor_scalar(desc[:, NG:NG + NE], iota[:, 0:NE], -1.0, float(NE), ALU.mult, ALU.add)
            pool.tensor_scalar(thr[:], iota[0:NE, 0:8], float(WIN), float(WIN), ALU.mult, ALU.add)
            pool.drain().then_inc(sem("consts"), 1)

            pool.wait_ge(*event("small_in", 16 * 20))
            pool.tensor_copy(abh[:], abw)
            pool.drain()
            pool.tensor_tensor(abl[:], abw, abh[:], ALU.subtract).then_inc(sem("ab_parts"), 1)

            def lo(p, t):
                pool.wait_ge(*event("w_hi", t + 1))
                pool.tensor_tensor(wl[p][:], slot[p], wh[p][:], ALU.subtract).then_inc(sem("w_lo"), 1)

            lo(0, 0)
            lo(1, 1)
            for i in range(8):
                t, k = i // 4, 4 * (i % 4)
                pool.wait_ge(*event("x_hi", i + 1))
                pool.tensor_tensor(xl[:, k:k + 4, t * P:t * P + P], xnT[:, k:k + 4, t * P:t * P + P],
                                   xh[:, k:k + 4, t * P:t * P + P], ALU.subtract).then_inc(sem("x_lo"), 1)
            lo(2, 2)
            lo(3, 3)
            for s in range(8):
                lo(s % PAIRS, PRO + s)
            with pool.Fori(1, NH) as h:
                for s in range(8):
                    lo(s % PAIRS, 8 * h + s + PRO)

            def gates_lo(f):
                for b in range(3):
                    lo(b, 3 * f + b + PRO + 8 * NH)

            gates_lo(0)
            with pool.Fori(1, KT) as f:
                gates_lo(f)

            for t in range(TT):
                pool.wait_ge(*event("h_hi", t + 1))
                pool.tensor_tensor(h_lo[:, t, :, :], h_tok[:, t, :, :], h_hi[:, t, :, :], ALU.subtract)\
                    .then_inc(sem("h_lo"), 1)

        @block.tensor
        def _(pe):
            mm = pe.matmul

            pe.wait_ge(*event("small_in", 16 * 20))
            pe.wait_ge(*event("consts", 1))
            mm(bank[6][:, 0:60], ones[0:1, :], rows[0:1, 0:60], start=True, stop=True).then_inc(sem("rows_bc"), 1)
            pe.wait_ge(*event("ident", 1))

            def transposes(src, ready, evac, base):
                for i in range(8):
                    t, k = i // 4, 4 * (i % 4)
                    if i % 4 == 0:
                        pe.wait_ge(*event(ready, base // 4 + t + 1))
                    if i >= 4:
                        pe.wait_ge(*event(evac, base + i - 3))
                    for j in range(4):
                        m = pe.transpose(bank[2 + i % 4][:, j * P:j * P + P], src(t, k + j), ident[:])
                    m.then_inc(sem(evac + "_in"), 1)

            transposes(lambda t, k: x_n[:, t, k * P:k * P + P], "x_n", "xnT", 0)
            pe.wait_ge(*event("x_lo", 8))
            pe.wait_ge(*event("ab_parts", 1))
            for i, (w_, x_) in enumerate(((abh, xh), (abh, xl), (abl, xh))):
                for k in range(KT):
                    m = mm(bank[7][0:16, 0:S], w_[:, k, :], x_[:, k, :], start=(i + k == 0), stop=(i == 2 and k == KT - 1))
            m.then_inc(sem("abT"), 1)

            def tile(to, p, t, part=0, parts=1):
                steps = [(wh[p], x_, k) for k in range(KT) for x_ in (xh, xl)] + [(wl[p], xh, k) for k in range(KT)]
                n = len(steps) // parts
                if part == 0:
                    pe.wait_ge(*event("w_hi", t + 1))
                for i in range(part * n, part * n + n):
                    w_, x_, k = steps[i]
                    if i == 2 * KT:
                        pe.wait_ge(*event("w_lo", t + 1))
                    m = mm(to, w_[:, k, :], x_[:, k, :], start=(i == 0), stop=(i == len(steps) - 1))
                return m

            for g in range(2):
                tile(bank[0][:, g * S:g * S + S], g, g).then_inc(sem("tile_mm"), 1)
            pe.wait_ge(*event("abT_sb", 1))
            pe.wait_ge(*event("rb", 1))
            for t in range(TT):
                m = pe.transpose(bank[6][:, 64 + 16 * t:80 + 16 * t], abT[0:16, t * P:t * P + P], ident[0:16, 0:16])
            m.then_inc(sem("ab_tok"), 1)
            for g in range(2):
                tile(bank[1][:, g * S:g * S + S], 2 + g, 2 + g).then_inc(sem("tile_mm"), 1)
            pe.wait_ge(*event("ksw_sq", 1))
            mm(bank[2][:], ones[:], sq_sb, start=True, stop=True).then_inc(sem("ksw_ss"), 1)
            pe.wait_ge(*event("v_raw", 1))
            for i in range(2 * TT):
                m = pe.transpose(bank[3][:, i * P:i * P + P], sq_dn[:, i * P:i * P + P], ident[:])
            m.then_inc(sem("vT"), 1)
            pe.wait_ge(*event("g", 1))
            mm(bank[7][:, 0:16], cumc[:], gt[:, 4, :], start=True, stop=True)
            mm(bank[7][:, 16:32], sufc[:], gt[:, 4, :], start=True, stop=True).then_inc(sem("gc"), 1)
            for i in range(8):
                pe.wait_ge(*event("diag", i + 1))
                if i >= 2:
                    pe.wait_ge(*event("diag_bc", i - 1))
                mm(bank[4 + i % 2][:], ones[:], (cv if i % 2 == 0 else ex)[:, 0:512], start=True, stop=True)\
                    .then_inc(sem("diag_mm"), 1)

            def dense(h, q):
                s = q // 4
                if q % 4 == 0 and not (isinstance(h, int) and 8 * h + s < 2):
                    pe.wait_ge(*event("raw", 8 * h + s - 1))
                m = tile(bank[s % 2][:, 0:S], s % PAIRS, 8 * h + s + PRO, q % 4, 4)
                if q % 4 == 3:
                    m.then_inc(sem("tile_mm"), 1)

            def mix(m, n, dense):
                for q in range(4):
                    dense(q)
                pe.wait_ge(*event("sb_sq", n))
                mm(bank[2][:], ones[:], sq_sb, start=True, stop=True).then_inc(sem("sb_ss"), 1)
                for t in range(TT):
                    m_ = pe.transpose(bank[5][:, t * P:t * P + P], raw_v[:, t * P:t * P + P], ident[:])
                m_.then_inc(sem("sb_vT"), 1)
                dense(4)
                pe.wait_ge(*event("dn_sq", n))
                pe.wait_ge(*event("sb_rt", n))
                mm(bank[2][:], ones[:], sq_dn, start=True, stop=True).then_inc(sem("dn_ss"), 1)
                dense(5)
                pe.wait_ge(*event("dn_rt", n))
                pe.wait_ge(*event("sw_sq", n))
                mm(bank[2][:, 0:S], ones[:], sq_sw, start=True, stop=True).then_inc(sem("sw_ss"), 1)
                dense(6)
                dense(7)
                pe.wait_ge(*event("sb_qk", n))
                kk = qk_sb[:, S:2 * S]
                mm(bank[3][:, 0:S], kk[:, 0:P], qk_sb[:, 0:S], start=True, stop=False, skip_group_check=True)
                mm(bank[3][:, S:S + P], kk[:, P:S], qk_sb[:, P:S], start=False, stop=False, skip_group_check=True)\
                    .then_inc(sem("sb_z"), 1)
                dense(8)
                pe.wait_ge(*event("dn_qk", n))
                for t in range(TT):
                    pe.transpose(bank[6][:, t * P:t * P + P], qk_dn[:, S + t * P:S + t * P + P], ident[:])
                for t in range(TT):
                    m_ = pe.transpose(bank[6][:, S + t * P:S + t * P + P], cv[:, 2 * S + t * P:2 * S + t * P + P], ident[:])
                m_.then_inc(sem("dn_kv"), 1)
                for t in range(TT):
                    mm(bank[7][:, t * P:t * P + P], qk_dn[:, S + t * P:S + t * P + P], qk_dn[:, S + t * P:S + t * P + P],
                       start=True, stop=True)
                for t in range(TT):
                    m_ = mm(bank[7][:, S + t * P:S + t * P + P], qk_dn[:, S + t * P:S + t * P + P],
                            qk_dn[:, t * P:t * P + P], start=True, stop=True)
                m_.then_inc(sem("dn_kk"), 1)
                dense(9)
                pe.wait_ge(*event("sw_q", n))
                kT = kT_sw[:, ds(m // 4, 1), :].rearrange("p a s -> p (a s)")
                mm(bank[4][:, 0:P], q_sw[:, 0:P], kT[:, 0:P], start=True, stop=True)
                mm(bank[4][:, P:3 * P], q_sw[:, P:S], kT[:, 0:S], start=True, stop=True).then_inc(sem("sw_s"), 1)
                dense(10)
                pe.wait_ge(*event("sb_sp", n))
                mm(bank[3][:, 0:S], negL[:], sp[:, 0:S], start=False, stop=False, skip_group_check=True)
                mm(bank[3][:, P:S], nones[:], sp[:, S:S + P], start=False, stop=False, skip_group_check=True)
                mm(bank[3][:, S:S + P], negL[:], sp[:, S:S + P], start=False, stop=True, skip_group_check=True)\
                    .then_inc(sem("sb_arg"), 1)
                dense(11)
                pe.wait_ge(*event("dn_round", 6 * n - 5))
                for t in range(TT):
                    m_ = pe.transpose(bank[7][:, t * P:t * P + P], pttt[:, t * S:t * S + P], ident[:])
                m_.then_inc(sem("dn_p"), 1)
                dense(12)
                pe.wait_ge(*event("sw_pr", n))
                for b in range(3):
                    m_ = pe.transpose(bank[4][:, b * P:b * P + P], smx[:, b * P:b * P + P], ident[:])
                m_.then_inc(sem("sw_prT"), 1)
                for r in range(6):
                    dense(13 + r)
                    pe.wait_ge(*event("dn_round", 6 * n - 5 + r))
                    pe.wait_ge(*event("dn_roundp", 6 * n - 5 + r))
                    for t in range(TT):
                        c = t * S + (P if r == 5 else 0)
                        m_ = mm(bank[6][:, c:t * S + S], pm[:, t * P:t * P + P], pttt[:, c:t * S + S], start=True, stop=True)
                    if r < 5:
                        for t in range(TT):
                            m_ = mm(bank[7][:, t * P:t * P + P], pttt[:, t * S:t * S + P], pm[:, t * P:t * P + P],
                                    start=True, stop=True)
                    m_.then_inc(sem("dn_sqr"), 1)
                    if r == 0:
                        pe.wait_ge(*event("sw_pT", n))
                        pe.wait_ge(*event("sb_v", n))
                        mm(bank[5][:, 0:S], v_sw[:, 0:P], pT[:, 0:S], start=True, stop=False, skip_group_check=True)
                        mm(bank[5][:, P:S], v_sw[:, P:S], pT[:, S:3 * P], start=False, stop=True, skip_group_check=True)\
                            .then_inc(sem("sw_av"), 1)
                    if r == 1:
                        pe.wait_ge(*event("sb_a", n))
                        pe.wait_ge(*event("sw_out", n))
                        mm(bank[5][:, S:2 * S], v_sb[:, 0, :], am[:, 0:S], start=True, stop=False, skip_group_check=True)
                        mm(bank[5][:, S + P:2 * S], v_sb[:, 1, :], am[:, S:3 * P], start=False, stop=True,
                           skip_group_check=True).then_inc(sem("sb_av"), 1)
                dense(19)
                pe.wait_ge(*event("dn_T", n))
                pe.wait_ge(*event("dn_kbg", n))
                for t in range(TT):
                    m_ = mm(bank[7][:, t * P:t * P + P], kbg[:, t * P:t * P + P], pttt[:, t * S + P:t * S + S],
                            start=True, stop=True)
                m_.then_inc(sem("dn_w"), 1)
                dense(20)
                for c in range(NCH):
                    t, r0 = c // 2, CH * (c % 2)
                    r = slice(r0, r0 + CH)
                    cc = slice(c * CH, c * CH + CH)
                    m_ = mm(bank[6][r, t * P:t * P + P], pttt[:, t * S + P + r0:t * S + P + r0 + CH],
                            vb[:, t * P:t * P + P], start=True, stop=(c == 0))
                    if c:
                        pe.wait_ge(*event("dn_state", 3 * n - 3 + c))
                        m_ = mm(bank[6][r, t * P:t * P + P], nwT[:, cc], state, start=False, stop=True)
                    m_.then_inc(sem("dn_v"), 1)
                    if c:
                        mm(bank[4][:, cc], state, eG[:, cc], start=True, stop=False)
                    dense(21 + 2 * c)
                    pe.wait_ge(*event("dn_vn", 4 * n - 3 + c))
                    m_ = mm(bank[4][:, cc], vn[r, t * P:t * P + P], attnT[r, t * P + r0:t * P + r0 + CH],
                            start=(c == 0), stop=True)
                    if c < NCH - 1:
                        if c == 0:
                            pe.wait_ge(*event("dn_nw", n))
                        m_ = mm(bank[7][:, S:S + P], kdec[r, t * P:t * P + P], vn[r, t * P:t * P + P], start=True, stop=True)
                    m_.then_inc(sem("dn_ds"), 1)
                    dense(22 + 2 * c)
                dense(29)
                dense(30)
                dense(31)
                pe.wait_ge(*event("dn_osq", n))
                mm(bank[2][:, 0:S], ones[:], sq_dn[:, 0:S], start=True, stop=True).then_inc(sem("dn_oss"), 1)

            pe.wait_ge(*event("kT_sw", 1))
            pe.wait_ge(*event("v_raw", 1))
            for q in range(32):
                dense(0, q)
            with pe.Fori(1, NH) as h:
                mix(h - 1, h, lambda q: dense(h, q))

            def first_gates(q):
                if 12 <= q < 28 and q % 2 == 0:
                    b, part = (q - 12) // 8, (q - 12) // 2 % 4
                    if part == 0:
                        pe.wait_ge(*event("raw", 8 * NH + b - 1))
                    m = tile(bank[b][:, 0:S], b, PRO + 8 * NH + b, part, 4)
                    if part == 3:
                        m.then_inc(sem(f"gused{b}"), 1)

            mix(NH - 1, NH, first_gates)

            pe.wait_ge(*event("head", NH + 1))

            def gates(f, first):
                for b in range(3):
                    if not first:
                        pe.wait_ge(*event(f"gsig{b}", f))
                    if not first or b == 2:
                        tile(bank[b][:, 0:S], b, 3 * f + b + PRO + 8 * NH).then_inc(sem(f"gused{b}"), 1)
                    pe.wait_ge(*event(f"bfull{b}", (f + 1) * 16))
                    if not first:
                        pe.wait_ge(*event("merged", f))
                    for k in range(8):
                        m = mm(bank[3 + b][:, 0:S], br_slot[b][:, k, :], outs[:, b, k, :], start=(k == 0), stop=(k == 7))
                    m.then_inc(sem(f"bused{b}"), 1)

            gates(0, True)
            with pe.Fori(1, KT) as f:
                gates(f, False)

            pe.wait_ge(*event("merged", KT))
            for n in range(4):
                for t in range(TT):
                    i = 2 * n + t
                    if t == 0:
                        pe.wait_ge(*event(f"wofull{n}", 16))
                    if i >= 2:
                        pe.wait_ge(*event("x1", i - 1))
                    for k in range(KT):
                        m = mm(bank[6 + t][:], merged[:, k, t * P:t * P + P], wo_slot[n][:, k, :],
                               start=(k == 0), stop=(k == KT - 1))
                    m.then_inc(sem("wo_mm"), 1)

            transposes(lambda t, k: h_tok[:, t, k, :], "h_tok", "hT", 0)
            pe.wait_ge(*event("hT", 8))
            for t in range(TT):
                for k in range(KT):
                    m = mm(bank[6][:, t * 36:t * 36 + 36], xnT[:, k, t * P:t * P + P], wr[:, k, :],
                           start=(k == 0), stop=(k == KT - 1))
            m.then_inc(sem("logits"), 1)
            pe.wait_ge(*event("chosen", 1))
            O = rt[:, 6]
            mm(bank[7][:, 0:32], upper[:], O[:, 0, :], start=True, stop=False, skip_group_check=True)
            mm(bank[7][:, 32:64], upper[:], O[:, 1, :], start=False, stop=False, skip_group_check=True)
            mm(bank[7][:, 32:64], ones[:], O[:, 0, :], start=False, stop=False, skip_group_check=True)
            mm(bank[6][0:NE, 128:256], O[:, 0, :], ones[:], start=True, stop=False)
            mm(bank[6][0:NE, 128:256], O[:, 1, :], ones[:], start=False, stop=True).then_inc(sem("counts"), 1)
            pe.wait_ge(*event("windows", 1))
            for t in range(TT):
                mm(bank[7][:, t * 32:t * 32 + 32], cntb, upper[0:NE, 0:NE], start=False, stop=(t == 1),
                   skip_group_check=True)
            mm(bank[2][:, 0:32], cntb, upper[0:NE, 0:NE], start=True, stop=True)
            mm(bank[2][:, 32:64], nwb, upper[0:NE, 0:NE], start=True, stop=True)
            mm(bank[2][:, 64:96], nwb, ident[0:NE, 0:NE], start=True, stop=True).then_inc(sem("slots"), 1)
            pe.wait_ge(*event("sel", 1))
            pe.wait_ge(*event("h_lo", 2))
            for k in range(KT):
                if k >= 4:
                    pe.wait_ge(*event("gathered", k - 3))
                for t in range(TT):
                    mm(bank[2 + k % 4][:], h_hi[:, t, k, :], sel[:, t, :], start=(t == 0), stop=False)
                    m = mm(bank[2 + k % 4][:], h_lo[:, t, k, :], sel[:, t, :], start=False, stop=(t == 1))
                m.then_inc(sem("gather_mm"), 1)

            def combine(v, t):
                if t == 0:
                    pe.wait_ge(*event("y", v))
                pe.wait_ge(*event("x2", 2 * v - 1 + t))
                for j in range(4):
                    m = mm(bank[4 + j][:], swT[32 * j:32 * j + 32, t, :], ysb[32 * j:32 * j + 32, :], start=True, stop=True)
                return m

            def window(v, full, last):
                pe.wait_ge(*event("xw", v))
                pe.wait_ge(*event("hidden", v))
                for i, b in ((0, 0), (1, 0), (2, 1), (3, 1)):
                    pe.wait_ge(*event(f"mfull{i}", full))
                    for k in range(8):
                        for j in range(4):
                            m = mm(bank[b][32 * j:32 * j + 32, 0:P], xw[:, 8 * (i % 2) + k, :],
                                   m_gu[i][:, k, j * P:j * P + P], start=(i % 2 == 0 and k == 0),
                                   stop=(i % 2 == 1 and k == 7))
                            if last and i == 2 and k == 0 and j == 0:
                                m.then_inc(sem("mused1"), 1)
                    if i % 2 == 1:
                        m.then_inc(sem(("gate_mm", "up_mm")[i // 2]), 1)
                        combine(v, i // 2).then_inc(sem("c_mm"), 1)
                    elif last:
                        m.then_inc(sem(f"mused{i}"), 1)
                pe.wait_ge(*event("sw", v))
                for t in range(TT):
                    m = pe.transpose(bank[2][:, t * P:t * P + P], sw[:, t, :], ident[:])
                    if last and t == 0:
                        m.then_inc(sem("mused3"), 1)
                m.then_inc(sem("swT_mm"), 1)
                pe.wait_ge(*event("swT", v))
                pe.wait_ge(*event("hidden", v + 1))
                pe.transpose(bank[2][:, S:S + P], hh, ident[:]).then_inc(sem("hT_mm"), 1)
                pe.wait_ge(*event("hidT", v))
                for i in range(2):
                    pe.wait_ge(*event(f"mfull{4 + i}", full))
                    for a in range(2):
                        for j in range(4):
                            c = 2 * i + a
                            m = mm(bank[3][32 * j:32 * j + 32, :], hT[:, 32 * c:32 * c + 32],
                                   m_down[i][:, 0, a, j * 512:j * 512 + 512], start=(c == 0), stop=(c == 3))
                    if i == 1:
                        m.then_inc(sem("y_mm"), 1)
                    elif last:
                        m.then_inc(sem("mused4"), 1)

            def expert(e, e1):
                more = pe.value_load(jobs[0:1, 0, ds(e, 1)], min_val=0, max_val=7)
                w0 = pe.value_load(jobs[0:1, 1, ds(e, 1)], min_val=0, max_val=64)
                with pe.If(more > 0):
                    with pe.Fori(0, more) as w:
                        window(w0 + w + 1, e1 * 16, False)
                window(w0 + more + 1, e1 * 16, True)

            pe.wait_ge(*event("jobs", 1))
            with pe.Fori(0, NE) as e:
                expert(e, e + 1)
            more = pe.value_load(jobs[0:1, 0, NE - 1:NE], min_val=0, max_val=7)
            w0 = pe.value_load(jobs[0:1, 1, NE - 1:NE], min_val=0, max_val=64)
            for t in range(TT):
                combine(w0 + more + 2, t).then_inc(sem("c_mm"), 1)

            pe.wait_ge(*event("p_in", 48))
            for j in range(2):
                for t in range(TT):
                    m = pe.transpose(bank[0][:, (2 * j + t) * P:(2 * j + t) * P + P], pin[:, t, j * P:j * P + P], ident[:])
            m.then_inc(sem("pT_mm"), 1)
            pe.wait_ge(*event("pT", 1))
            for i in range(8):
                n, t = i // 2, i % 2
                if i >= 4:
                    pe.wait_ge(*event("pple", i - 3))
                for j in range(2):
                    m = mm(bank[i % 4][:], kT_sw[:, j, t * P:t * P + P], wpp[:, j, n * 512:n * 512 + 512],
                           start=(j == 0), stop=(j == 1))
                m.then_inc(sem("pple_mm"), 1)
            pe.wait_ge(*event("pple", 8))
            transposes(lambda t, k: x3n[:, t, k * P:k * P + P], "x3n", "x3T", 0)
            pe.wait_ge(*event("x3T", 8))
            for n in range(4):
                pe.wait_ge(*event(f"plfull{n % 3}", 16 * (n // 3 + 1)))
                for t in range(TT):
                    i = 2 * n + t
                    if i >= 2:
                        pe.wait_ge(*event("ple_sig", i - 1))
                    for k in range(KT):
                        m = mm(bank[6 + t][:], x3T[:, k, t * P:t * P + P], pl_slot[n % 3][:, k, :],
                               start=(k == 0), stop=(k == KT - 1))
                    m.then_inc(sem("gple_done"), 1)

        def bc(ap, shape):
            return ap.to_broadcast(shape)

        @block.scalar
        def _(act):
            def f(out, in_, func, **kw):
                return act.activation(out, in_, func, **kw)

            def load_exp_ln():
                act.add_instruction(mybir.InstLoadActFuncSet(act_func_set_id=EXP_LN_SET, name=nc.get_next_instruction_name(),
                                                             engine=mybir.EngineType.Activation))

            def inverse_root(to, of, scale):
                f(to, of, ACT.Ln, scale=scale, bias=epsb[:, 0:1])
                act.drain()
                return f(to, to, ACT.Exp, scale=-0.5)

            load_exp_ln()

            def mean_squares(ready):
                for t in range(TT):
                    f(dump, x_tok[:, t, :], ACT.Square, accum_out=rs2[:, t:t + 1])
                    act.drain()
                inverse_root(rs2[:, 4:6], rs2[:, 0:2], 1.0 / D).then_inc(sem(ready), 1)

            act.wait_ge(*event("x_in", 16))
            act.wait_ge(*event("eps", 1))
            mean_squares("x_rms")

            def hi(h, s):
                p, before = s % PAIRS, 0 if isinstance(h, int) and h < 0 else 1 + 2 * h + s // PAIRS
                act.wait_ge(*event(f"full{p}", 16 * (before + 1)))
                f(wh[p][:], slot[p], ACT.Copy).then_inc(sem("w_hi"), 1)

            hi(-1, 0)
            hi(-1, 1)
            for i in range(8):
                t, k = i // 4, 4 * (i % 4)
                act.wait_ge(*event("xnT", i + 1))
                f(xh[:, k:k + 4, t * P:t * P + P], xnT[:, k:k + 4, t * P:t * P + P], ACT.Copy).then_inc(sem("x_hi"), 1)
            hi(-1, 2)
            hi(-1, 3)
            act.wait_ge(*event("abT", 1))
            f(abT[0:16, :], bank[7][0:16, 0:S], ACT.Copy).then_inc(sem("abT_sb"), 1)
            act.wait_ge(*event("tile_mm", 2))
            f(sq_sb, bank[0][:], ACT.Square).then_inc(sem("ksw_sq"), 1)
            hi(0, 0)
            act.wait_ge(*event("ksw_ss", 1))
            inverse_root(r_sb, bank[2][:], 1.0 / P).then_inc(sem("ksw_rt"), 1)
            hi(0, 1)
            act.wait_ge(*event("tile_mm", 4))
            f(sq_dn, bank[1][:], ACT.Copy).then_inc(sem("v_raw"), 1)
            act.wait_ge(*event("vT", 1))
            f(vt_sw, bank[3][:].rearrange("p (g n) -> p g n", g=2), ACT.Copy).then_inc(sem("vt_sw"), 1)
            act.wait_ge(*event("ab_v", 1))
            f(gt[:, 1, :], gt[:, 0, :], ACT.Abs)
            f(gt[:, 3, 0:8], rb[:, 8:16], ACT.Exp)
            f(gt[:, 5, :].rearrange("p (t h) -> p t h", t=TT), ab_psum[:, :, 8:16], ACT.Exp, scale=-1.0)
            act.drain()
            f(gt[:, 1, :], gt[:, 1, :], ACT.Exp, scale=-1.0)
            act.drain()
            f(gt[:, 1, :], gt[:, 1, :], ACT.Ln, bias=1.0).then_inc(sem("ab_sp"), 1)
            act.wait_ge(*event("gc_sb", 1))
            f(gt[:, 1, :], gt[:, 6, :], ACT.Exp)
            f(head[:, F_KD:F_KD + 2, :], gt[:, 7, :].rearrange("p (t h) -> p t h", t=TT), ACT.Exp)\
                .then_inc(sem("gc_exp"), 1)
            for i in range(0, 8, 2):
                act.wait_ge(*event("diag_mm", i + 1))
                t, hq = i // 4, (i // 2) % 2
                f(Gb[:, 4 * hq:4 * hq + 4, t * P:t * P + P], bank[4][:].rearrange("p (h n) -> p h n", h=4), ACT.Copy)
                act.drain().then_inc(sem("Gb"), 1)
            f(head[:, F_EGL:F_EGL + 4, :], Gb.rearrange("p h (c s) -> p c h s", c=NCH)[:, :, :, CH - 1], ACT.Exp)\
                .then_inc(sem("egl"), 1)

            def evacuate(s, h):
                to = (raw_dn[:, 0, 3:], raw_dn[:, 1, 3:], raw_dn[:, 2, 3:], raw_v, raw_sb[:, 0, :], raw_sb[:, 1, :],
                      raw_z, raw_sw)[s]
                act.wait_ge(*event("tile_mm", 8 * h + s + PRO + 1))
                f(to, bank[s % 2][:, 0:S], ACT.Copy).then_inc(sem("raw"), 1)

            def mix(n, evac, hi, sigmoid_conv):
                act.drain()
                act.wait_ge(*event("head", n))
                f(sq_sb, raw_sb[:, :, :].rearrange("p a s -> p (a s)"), ACT.Square).then_inc(sem("sb_sq"), 1)
                act.wait_ge(*event("dn_silu", n))
                f(sq_dn, cv[:, 0:2 * S], ACT.Square).then_inc(sem("dn_sq"), 1)
                f(sq_sw, raw_sw, ACT.Square).then_inc(sem("sw_sq"), 1)
                evac(0)
                hi(2)
                load_exp_ln()
                act.wait_ge(*event("sb_ss", n))
                inverse_root(r_sb, bank[2][:], 1.0 / P).then_inc(sem("sb_rt"), 1)
                act.wait_ge(*event("dn_ss", n))
                inverse_root(r_dn, bank[2][:], 1.0).then_inc(sem("dn_rt"), 1)
                act.wait_ge(*event("sw_ss", n))
                inverse_root(r_sw, bank[2][:, 0:S], 1.0 / P).then_inc(sem("sw_rt"), 1)
                act.wait_ge(*event("sb_vT", n))
                f(v_sb, bank[5][:, 0:S].rearrange("p (t n) -> p t n", t=TT), ACT.Copy).then_inc(sem("sb_v"), 1)
                hi(3)
                evac(1)
                act.wait_ge(*event("sb_z", n))
                f(za, bank[3][:, 0:384], ACT.Abs)
                act.drain()
                f(za, za, ACT.Exp, scale=-1.0)
                act.drain()
                f(za, za, ACT.Ln, bias=1.0).then_inc(sem("sb_ln"), 1)
                act.wait_ge(*event("dn_diff", n))
                f(decT, decT, ACT.Exp).then_inc(sem("dn_dec"), 1)
                f(eG, Gb[:, ds(n - 1, 1), :].rearrange("p a s -> p (a s)"), ACT.Exp).then_inc(sem("dn_eg"), 1)
                act.wait_ge(*event("dn_kv", n))
                for t in range(TT):
                    f(kbg[:, t * P:t * P + P], bank[6][:, t * P:t * P + P], ACT.Copy, scale=hs[:, F_BEG + t:F_BEG + t + 1])
                    f(vb[:, t * P:t * P + P], bank[6][:, S + t * P:S + t * P + P], ACT.Copy,
                      scale=hs[:, F_BETA + t:F_BETA + t + 1])
                    i = f(kdec[:, t * P:t * P + P], bank[6][:, t * P:t * P + P], ACT.Copy,
                          scale=hs[:, F_KD + t:F_KD + t + 1])
                i.then_inc(sem("dn_kbg"), 1)
                hi(4)
                act.wait_ge(*event("sw_max", n))
                f(smx[:, 0:P], smx[:, 0:P], ACT.Exp, bias=sm[:, 2:3], accum_out=sm[:, 4:5])
                f(smx[:, P:3 * P], smx[:, P:3 * P], ACT.Exp, bias=sm[:, 3:4], accum_out=sm[:, 5:6])
                f(sm[:, 6:8], sm[:, 2:4], ACT.Exp, bias=hs[:, F_SINK:F_SINK + 1]).then_inc(sem("sw_exp"), 1)
                act.wait_ge(*event("sb_amin", n))
                f(am, am, ACT.Exp).then_inc(sem("sb_a"), 1)
                evac(2)
                act.wait_ge(*event("dn_p", n))
                f(pm, bank[7][:, 0:S], ACT.Copy).then_inc(sem("dn_roundp"), 1)
                act.wait_ge(*event("sw_prT", n))
                f(pT, bank[4][:, 0:384], ACT.Copy).then_inc(sem("sw_pT"), 1)
                hi(5)
                for r in range(5):
                    act.wait_ge(*event("dn_sqr", 6 * n - 5 + r))
                    f(pm, bank[7][:, 0:S], ACT.Copy).then_inc(sem("dn_roundp"), 1)
                    if r == 0:
                        act.wait_ge(*event("sw_av", n))
                        f(outs[:, 0, ds(n - 1, 1), :].rearrange("p a s -> p (a s)"), bank[5][:, 0:S], ACT.Copy)\
                            .then_inc(sem("sw_out"), 1)
                    if r == 3:
                        hi(6)
                    if r == 4:
                        f(ez, raw_z, ACT.Sigmoid).then_inc(sem("z_sig"), 1)
                        sigmoid_conv()
                    if r == 2:
                        evac(3)
                        act.wait_ge(*event("sb_av", n))
                        f(outs[:, 1, ds(n - 1, 1), :].rearrange("p a s -> p (a s)"), bank[5][:, S:2 * S], ACT.Copy)\
                            .then_inc(sem("sb_out"), 1)
                act.wait_ge(*event("dn_w", n))
                f(nwT, bank[7][:, 0:S], ACT.Copy, scale=-1.0).then_inc(sem("dn_nw"), 1)
                evac(4)
                hi(7)
                evac(5)
                hi(8)
                act.wait_ge(*event("dn_sz", n))
                evac(6)
                act.wait_ge(*event("dn_ds", 4 * n))
                f(sq_dn[:, 0:S], bank[4][:, 0:S], ACT.Square).then_inc(sem("dn_osq"), 1)
                evac(7)
                act.wait_ge(*event("dn_oss", n))
                inverse_root(r_dn[:, 0:S], bank[2][:, 0:S], 1.0 / P).then_inc(sem("dn_ort"), 1)
                hi(9)

            def conv_sig(n):
                act.wait_ge(*event("dn_conv", n))
                f(ex, cv, ACT.Sigmoid).then_inc(sem("dn_sig"), 1)

            for s in range(8):
                hi(0, s + 2)
                evacuate(s, 0)
                if s == 5:
                    conv_sig(1)
            with act.Fori(1, NH) as h:
                mix(h, lambda s: evacuate(s, h), lambda s: hi(h, s), lambda: conv_sig(h + 1))
            mix(NH, lambda s: None, lambda s: hi(NH, s) if s == 2 else None, lambda: None)

            def gate_hi(b, t):
                act.wait_ge(*event(f"gfull{b}", 16 * (t + 1)))
                f(wh[b][:], slot[b], ACT.Copy).then_inc(sem("g_hi"), 1)

            def gates(f1, more):
                for b in range(3):
                    act.wait_ge(*event(f"gused{b}", f1))
                    f(esig[b], bank[b][:, 0:S], ACT.Sigmoid).then_inc(sem(f"gsig{b}"), 1)
                    if more:
                        gate_hi(b, f1)

            gates(1, True)
            with act.Fori(2, KT) as f1:
                act.wait_ge(*event("merged", f1 - 1))
                gates(f1, True)
            act.wait_ge(*event("merged", KT - 1))
            gates(KT, False)

            load_exp_ln()
            act.wait_ge(*event("x1", 8))
            mean_squares("x1_rms")
            act.wait_ge(*event("logits", 1))
            for t in range(TT):
                f(h_hi[:, t, :, :], h_tok[:, t, :, :], ACT.Copy).then_inc(sem("h_hi"), 1)
            act.wait_ge(*event("maxes", 1))
            f(rsm[:, 8, :], rsm[:, 7, :], ACT.Exp)
            for t in range(TT):
                f(lg[:, t, 0:NG], lg[:, t, 0:NG], ACT.Exp, bias=rsm[:, 6, t:t + 1], accum_out=rsm[:, 9, t:t + 1])
            act.drain().then_inc(sem("gexps"), 1)
            for k in range(1, KT, 2):
                act.wait_ge(*event("gather_mm", k + 1))
                act.wait_ge(*event("gathered", k))
                f(xs[:, k, 0:NSLOT], bank[2 + k % 4][:], ACT.Copy, scale=ngf[:, k:k + 1]).then_inc(sem("gathered"), 1)

            def window(v):
                act.wait_ge(*event("gate_mm", v))
                f(eg, bank[0][:, 0:P], ACT.Sigmoid).then_inc(sem("gate_sig"), 1)
                act.wait_ge(*event("swT_mm", v))
                f(swT, bank[2][:, 0:S].rearrange("p (t n) -> p t n", t=TT), ACT.Copy).then_inc(sem("swT"), 1)
                act.wait_ge(*event("hT_mm", v))
                f(hT, bank[2][:, S:S + P], ACT.Copy).then_inc(sem("hidT"), 1)
                act.wait_ge(*event("y_mm", v))
                f(ysb, bank[3][:], ACT.Copy).then_inc(sem("y"), 1)

            act.wait_ge(*event("jobs", 1))
            with act.Fori(0, NE) as e:
                more = act.value_load(jobs[0:1, 0, ds(e, 1)], min_val=0, max_val=7)
                w0 = act.value_load(jobs[0:1, 1, ds(e, 1)], min_val=0, max_val=64)
                with act.Fori(0, more + 1) as w:
                    window(w0 + w + 1)
                act.drain().then_inc(sem("mused5"), 1)

            load_exp_ln()
            act.wait_ge(*event("x2_all", 1))
            mean_squares("x3_rms")
            for i in range(8):
                act.wait_ge(*event("gple_done", i + 1))
                if i >= 2:
                    act.wait_ge(*event("result", i - 1))
                f(pe_e[i % 2], bank[6 + i % 2][:], ACT.Sigmoid).then_inc(sem("ple_sig"), 1)

        @block.vector
        def _(dve):
            tt, ts, stt = dve.tensor_tensor, dve.tensor_scalar, dve.scalar_tensor_tensor

            def nxt():
                dve.drain()

            dve.memset(epsb[:], EPS).then_inc(sem("eps"), 1)
            dve.memset(raw_dn[:, :, 0:3], 0.0)
            dve.wait_ge(*event("small_in", 16 * 20))
            for part in range(3):
                c = F_CONV + 4 * part
                dve.tensor_copy(head[:, c:c + 4, :], convw[:, 8 * part:8 * part + 8, :].rearrange("p h j -> p j h"))
            ts(gains[:, 5:6], gains[:, 2:3], HS, None, ALU.mult)
            ts(gains[:, 6:7], gains[:, 0:1], HS, None, ALU.mult)
            dve.wait_ge(*event("rows_bc", 1))
            dve.tensor_copy(rb[:, 0:60], bank[6][:, 0:60]).then_inc(sem("rb"), 1)
            nxt()
            dve.tensor_copy(head[:, F_SINK, :], rb[:, 16:24])
            dve.wait_ge(*event("iota", 1))

            def evac_T(to, evac, g):
                for i in range(8):
                    t, k = i // 4, 4 * (i % 4)
                    dve.wait_ge(*event(evac + "_in", i + 1))
                    tt(to[:, k:k + 4, t * P:t * P + P], bank[2 + i % 4][:].rearrange("p (k n) -> p k n", k=4),
                       bc(g[:, k:k + 4].unsqueeze(2), [P, 4, P]), ALU.mult).then_inc(sem(evac), 1)

            dve.wait_ge(*event("x_rms", 1))
            for t in range(TT):
                ts(x_n[:, t, :], x_tok[:, t, :], rs2[:, 4 + t:5 + t], None, ALU.mult).then_inc(sem("x_n"), 1)
            evac_T(xnT, "xnT", ng)
            dve.wait_ge(*event("ksw_rt", 1))
            stt(kT_sw[:].rearrange("p g s -> p (g s)"), bank[0][:], gains[:, 1:2], r_sb, ALU.mult, ALU.mult)\
                .then_inc(sem("kT_sw"), 1)
            dve.wait_ge(*event("ab_tok", 1))
            tth = lambda a: a.rearrange("p (t h) -> p t h", t=TT)
            g_ = lambda i: tth(gt[:, i, :])
            tt(g_(0), ab_psum[:, :, 0:8], bc(rb[:, 0:8].unsqueeze(1), [P, TT, 8]), ALU.add).then_inc(sem("ab_v"), 1)
            dve.wait_ge(*event("ab_sp", 1))
            stt(g_(2), g_(0), 0.0, g_(1), ALU.max, ALU.add)
            ts(gt[:, 5, :], gt[:, 5, :], 1.0, None, ALU.add)
            nxt()
            stt(g_(4), g_(2), -1.0, bc(gt[:, 3, 0:8].unsqueeze(1), [P, TT, 8]), ALU.mult, ALU.mult).then_inc(sem("g"), 1)
            dve.reciprocal(head[:, F_BETA:F_BETA + 2, :], g_(5))
            dve.wait_ge(*event("gc", 1))
            dve.tensor_copy(gt[:, 6:8, :].rearrange("p i n -> p (i n)"), bank[7][:, 0:32]).then_inc(sem("gc_sb"), 1)
            nxt()
            ts(head[:, F_NGC:F_NGC + 2, :], g_(6), -1.0, None, ALU.mult)
            dve.wait_ge(*event("gc_exp", 1))
            tt(head[:, F_BEG:F_BEG + 2, :], g_(1), head[:, F_BETA:F_BETA + 2, :], ALU.mult)
            def diag(i):
                t, hq, kind = i // 4, (i // 2) % 2, i % 2
                src = g_(6) if kind == 0 else head[:, F_BETA:F_BETA + 2, :]
                tt((cv, ex)[i % 2][:, 0:512].rearrange("p (h n) -> p h n", h=4),
                   bc(ident[:].unsqueeze(1), [P, 4, P]), bc(src[:, t, 4 * hq:4 * hq + 4].unsqueeze(2), [P, 4, P]),
                   ALU.mult).then_inc(sem("diag"), 1)

            def neg_beta(i):
                t, hq = i // 4, (i // 2) % 2
                tt(nBb[:, 4 * hq:4 * hq + 4, t * P:t * P + P], bank[5][:].rearrange("p (h n) -> p h n", h=4),
                   bc(nmask[:].unsqueeze(1), [P, 4, P]), ALU.mult).then_inc(sem("diag_bc"), 1)

            for i in range(8):
                if i >= 2:
                    dve.wait_ge(*event("diag_mm", i - 1))
                diag(i)
                if i >= 1:
                    j = i - 1
                    if j % 2 == 0:
                        dve.wait_ge(*event("Gb", j // 2 + 1))
                        dve.engine_nop().then_inc(sem("diag_bc"), 1)
                    else:
                        dve.wait_ge(*event("diag_mm", j + 1))
                        neg_beta(j)
            dve.wait_ge(*event("diag_mm", 8))
            neg_beta(7)
            dve.wait_ge(*event("egl", 1))
            dve.wait_ge(*event("vt_sw", 1))
            dve.drain().then_inc(sem("head"), 1)

            def tap(j, n):
                if j == 0:
                    dve.wait_ge(*event("raw", 8 * n - 5))
                    dve.tensor_copy(hc[:], head[:, F_CONV:NF, ds(n - 1, 1)].rearrange("p f a -> p (f a)"))
                nxt()
                for part in range(3):
                    o, w = cv[:, part * S:part * S + S], hc[:, 4 * part + j:4 * part + j + 1]
                    if j == 0:
                        ts(o, raw_dn[:, part, 0:S], w, None, ALU.mult)
                    else:
                        i = stt(o, raw_dn[:, part, j:j + S], w, o, ALU.mult, ALU.add)
                if j == 3:
                    i.then_inc(sem("dn_conv"), 1)

            def silu(n):
                dve.wait_ge(*event("dn_sig", n))
                tt(cv, cv, ex, ALU.mult).then_inc(sem("dn_silu"), 1)

            def mix(n, next_tap, next_silu):
                one = ds(n - 1, 1)
                dve.drain()
                dve.tensor_copy(hs[:], head[:, 0:F_CONV, one].rearrange("p f a -> p (f a)"))
                dve.tensor_copy(v_sw, vt_sw[:, ds((n - 1) // 4, 1), :].rearrange("p a s -> p (a s)"))
                nxt()
                dve.wait_ge(*event("sb_rt", n))
                stt(qk_sb[:, 0:S], raw_sb[:, 0, :], gains[:, 5:6], r_sb[:, 0:S], ALU.mult, ALU.mult)
                stt(qk_sb[:, S:2 * S], raw_sb[:, 1, :], gains[:, 3:4], r_sb[:, S:2 * S], ALU.mult, ALU.mult)\
                    .then_inc(sem("sb_qk"), 1)
                dve.wait_ge(*event("dn_rt", n))
                stt(qk_dn[:, 0:S], cv[:, 0:S], HS, r_dn[:, 0:S], ALU.mult, ALU.mult)
                tt(qk_dn[:, S:2 * S], cv[:, S:2 * S], r_dn[:, S:2 * S], ALU.mult).then_inc(sem("dn_qk"), 1)
                G = Gb[:, one, :].rearrange("p a s -> p (a s)")
                for t in range(TT):
                    i = stt(decT[:, t * P:t * P + P], G[:, t * P:t * P + P], hs[:, F_NGC + t:F_NGC + t + 1], capdn[:],
                            ALU.add, ALU.min)
                i.then_inc(sem("dn_diff"), 1)
                dve.wait_ge(*event("sw_rt", n))
                stt(q_sw, raw_sw, gains[:, 6:7], r_sw, ALU.mult, ALU.mult).then_inc(sem("sw_q"), 1)
                dve.wait_ge(*event("sb_ln", n))
                stt(sp, bank[3][:, 0:384], 0.0, za, ALU.max, ALU.add)
                nxt()
                spd = sp.rearrange("p (b n) -> p b n", b=3)[:, 0:3:2, :]
                tt(spd, spd, bc(upper[:].unsqueeze(1), [P, 2, P]), ALU.mult).then_inc(sem("sb_sp"), 1)
                dve.wait_ge(*event("sw_s", n))
                tt(smx, bank[4][:, 0:384], masksw[:].rearrange("p b n -> p (b n)"), ALU.add)
                nxt()
                dve.tensor_reduce(sm[:, 0:1], smx[:, 0:P], AX.X, ALU.max)
                dve.tensor_reduce(sm[:, 1:2], smx[:, P:3 * P], AX.X, ALU.max)
                nxt()
                ts(sm[:, 2:4], sm[:, 0:2], hs[:, F_SINK:F_SINK + 1], -1.0, ALU.max, ALU.mult).then_inc(sem("sw_max"), 1)
                dve.wait_ge(*event("dn_dec", n))
                dve.wait_ge(*event("dn_kk", n))
                p4 = pttt.rearrange("p (t a n) -> p t a n", t=TT, a=2)
                two = lambda a: a.rearrange("p (t n) -> p t n", t=TT)
                tt(attnT, bank[7][:, S:2 * S], decT, ALU.mult)
                tt(decT, bank[7][:, 0:S], decT, ALU.mult)
                nxt()
                tt(p4[:, :, 0, :], two(decT), nBb[:, one, :].rearrange("p a (t n) -> p (a t) n", t=TT), ALU.mult)
                dve.tensor_copy(p4[:, :, 1, :], bc(ident[:].unsqueeze(1), [P, TT, P])).then_inc(sem("dn_round"), 1)
                dve.wait_ge(*event("dn_eg", n))
                tt(eG, eG, qk_dn[:, 0:S], ALU.mult).then_inc(sem("decays_used"), 1)
                dve.wait_ge(*event("sb_arg", n))
                tt(am, bank[3][:, 0:384], capsb[:].rearrange("p b n -> p (b n)"), ALU.min).then_inc(sem("sb_amin"), 1)
                dve.wait_ge(*event("sw_exp", n))
                tt(sm[:, 8:10], sm[:, 4:6], sm[:, 6:8], ALU.add)
                nxt()
                dve.reciprocal(sm[:, 10:12], sm[:, 8:10])
                nxt()
                ts(smx[:, 0:P], smx[:, 0:P], sm[:, 10:11], None, ALU.mult)
                ts(smx[:, P:3 * P], smx[:, P:3 * P], sm[:, 11:12], None, ALU.mult).then_inc(sem("sw_pr"), 1)
                for r in range(6):
                    dve.wait_ge(*event("dn_sqr", 6 * n - 5 + r))
                    b6 = bank[6][:].rearrange("p (t a n) -> p t a n", t=TT, a=2)
                    if r < 5:
                        dve.tensor_copy(p4[:, :, 0, :], b6[:, :, 0, :])
                    i = tt(p4[:, :, 1, :], b6[:, :, 1, :], p4[:, :, 1, :], ALU.add)
                    i.then_inc(sem("dn_round" if r < 5 else "dn_T"), 1)
                    if r < 4:
                        next_tap(r)
                dve.wait_ge(*event("z_sig", n))
                tt(ez, ez, raw_z, ALU.mult).then_inc(sem("dn_sz"), 1)
                next_silu()
                for c in range(NCH):
                    t, r = c // 2, slice(CH * (c % 2), CH * (c % 2) + CH)
                    dve.wait_ge(*event("dn_v", 4 * n - 3 + c))
                    dve.tensor_copy(vn[r, t * P:t * P + P], bank[6][r, t * P:t * P + P]).then_inc(sem("dn_vn"), 1)
                    if c < NCH - 1:
                        dve.wait_ge(*event("dn_ds", 4 * n - 3 + c))
                        if c == 0:
                            i = dve.tensor_copy(state, bank[7][:, S:S + P])
                        else:
                            i = stt(state, state, hs[:, F_EGL + c:F_EGL + c + 1], bank[7][:, S:S + P], ALU.mult, ALU.add)
                        i.then_inc(sem("dn_state"), 1)
                dve.wait_ge(*event("dn_ort", n))
                tt(r_dn[:, 0:S], r_dn[:, 0:S], ez, ALU.mult)
                nxt()
                stt(outs[:, 2, one, :].rearrange("p a s -> p (a s)"), bank[4][:, 0:S], gains[:, 4:5], r_dn[:, 0:S],
                    ALU.mult, ALU.mult).then_inc(sem("head"), 1)

            for j in range(4):
                tap(j, 1)
            silu(1)
            with dve.Fori(1, NH) as h:
                mix(h, lambda j: tap(j, h + 1), lambda: silu(h + 1))
            mix(NH, lambda j: None, lambda: None)

            def gates(f1, at_):
                for b in range(3):
                    dve.wait_ge(*event(f"gsig{b}", f1))
                    dve.wait_ge(*event(f"bused{b}", f1))
                    i = tt(esig[b], esig[b], bank[3 + b][:, 0:S], ALU.mult)
                    if b:
                        nxt()
                        to = macc if b == 1 else merged[:, at_, :].rearrange("p a s -> p (a s)")
                        i = tt(to, esig[b], esig[0] if b == 1 else macc, ALU.add)
                i.then_inc(sem("merged"), 1)

            dve.wait_ge(*event("head", NH + 1))
            gates(1, ds(0, 1))
            with dve.Fori(2, KT + 1) as f1:
                gates(f1, ds(f1 - 1, 1))

            for i in range(8):
                n, t = i // 2, i % 2
                dve.wait_ge(*event("wo_mm", i + 1))
                o = x_tok[:, t, n * 512:n * 512 + 512]
                if i == 0:
                    dve.wait_ge(*event("x_in", 32))
                tt(o, o, bank[6 + t][:], ALU.add).then_inc(sem("x1"), 1)

            dve.wait_ge(*event("x1_rms", 1))
            for t in range(TT):
                ts(h_tok[:, t, :, :], x_tok[:, t, :].rearrange("p (c k) -> p k c", k=KT), rs2[:, 4 + t:5 + t], None,
                   ALU.mult).then_inc(sem("h_tok"), 1)
            evac_T(xnT, "hT", ngf)
            dve.wait_ge(*event("logits", 1))
            R = lambda i: rsm[:, i, :]
            b8 = lambda i, w: bc(rsm[:, i, :].unsqueeze(2), [P, TT, w])
            lp = bank[6][:, 0:72].rearrange("p (t n) -> p t n", t=TT)
            tt(lg[:], lp, bc(rb[:, 24:60].unsqueeze(1), [P, TT, 36]), ALU.add)
            nxt()
            g4 = rt[:, 0, :, 0:NG]
            dve.tensor_reduce(R(0), lg[:, :, 0:NG], AX.X, ALU.max)
            nxt()
            tt(g4, lg[:, :, 0:NG], b8(0, NG), ALU.is_equal)
            ts(R(6), R(0), -1.0, None, ALU.mult)
            nxt()
            tt(g4, g4, bc(desc[:, 0:NG].unsqueeze(1), [P, TT, NG]), ALU.mult)
            nxt()
            dve.tensor_reduce(R(1), g4, AX.X, ALU.max)
            nxt()
            tt(g4, bc(desc[:, 0:NG].unsqueeze(1), [P, TT, NG]), b8(1, NG), ALU.is_equal)
            nxt()
            gm = rt[:, 1, :, 0:NG]
            ts(gm, g4, 1.0, BIG, ALU.subtract, ALU.mult)
            nxt()
            el = rt[:, 2]
            for t in range(TT):
                e4 = el[:, t, :].rearrange("p (g e) -> p g e", g=NG)
                tt(e4, lg[:, t, NG:].rearrange("p (g e) -> p g e", g=NG), bc(g4[:, t, :].unsqueeze(2), [P, NG, EPG]), ALU.mult)
            nxt()
            for t in range(TT):
                e4 = el[:, t, :].rearrange("p (g e) -> p g e", g=NG)
                tt(e4, e4, bc(gm[:, t, :].unsqueeze(2), [P, NG, EPG]), ALU.add)
            nxt()

            def first_max(m, first, one_hot, scratch):
                dve.tensor_reduce(R(m), el, AX.X, ALU.max)
                nxt()
                tt(scratch, el, b8(m, NE), ALU.is_equal)
                nxt()
                tt(scratch, scratch, bc(desc[:, NG:].unsqueeze(1), [P, TT, NE]), ALU.mult)
                nxt()
                dve.tensor_reduce(R(first), scratch, AX.X, ALU.max)
                nxt()
                tt(one_hot, bc(desc[:, NG:].unsqueeze(1), [P, TT, NE]), b8(first, NE), ALU.is_equal)
                nxt()

            oh1, oh2 = rt[:, 3], rt[:, 4]
            first_max(2, 3, oh1, rt[:, 5])
            stt(el, oh1, -3e38, el, ALU.mult, ALU.add)
            nxt()
            first_max(4, 5, oh2, rt[:, 5])
            tt(R(7), R(4), R(2), ALU.subtract).then_inc(sem("maxes"), 1)
            O = rt[:, 6]
            tt(O, oh1, oh2, ALU.add).then_inc(sem("chosen"), 1)
            dve.wait_ge(*event("counts", 1))
            dve.tensor_copy(cntb, bank[6][0:NE, 128:256])
            nxt()
            tt(cmp8[:], bc(cntb[:, 0:1], [NE, 8]), thr[:], ALU.is_gt)
            nxt()
            dve.tensor_reduce(thr[:, 0:1], cmp8[:], AX.X, ALU.add)
            nxt()
            ts(nwb, bc(thr[:, 0:1], [NE, P]), 1.0, None, ALU.add).then_inc(sem("windows"), 1)
            dve.wait_ge(*event("gexps", 1))
            ts(R(10), R(8), 1.0, None, ALU.add)
            nxt()
            tt(R(10), R(10), R(9), ALU.mult)
            nxt()
            dve.reciprocal(R(11), R(10))
            nxt()
            tt(R(12), R(11), R(8), ALU.mult)
            nxt()
            tt(rt[:, 7], oh1, b8(11, NE), ALU.mult)
            tt(rt[:, 8], oh2, b8(12, NE), ALU.mult)
            nxt()
            tt(posw[:, 2:4, :], rt[:, 7], rt[:, 8], ALU.add)
            dve.wait_ge(*event("slots", 1))
            pos = bank[7][:, 0:64].rearrange("p (t e) -> p t e", t=TT)
            stt(rt[:, 9], pos, 1.0, O, ALU.add, ALU.mult)
            dve.tensor_copy(jobs[0:1, 2, :], bank[2][0:1, 0:32])
            dve.tensor_copy(jobs[0:1, 1, :], bank[2][0:1, 32:64])
            ts(jobs[0:1, 0, :], bank[2][0:1, 64:96], 1.0, None, ALU.subtract).then_inc(sem("jobs"), 1)
            nxt()
            ts(posw[:, 0:2, :], rt[:, 9], 1.0, None, ALU.subtract)
            tt(rt[:, 10], rt[:, 9], oh1, ALU.mult)
            tt(rt[:, 11], rt[:, 9], oh2, ALU.mult)
            nxt()
            dve.tensor_reduce(R(13), rt[:, 10], AX.X, ALU.add)
            dve.tensor_reduce(R(14), rt[:, 11], AX.X, ALU.add)
            nxt()
            ts(rsm[:, 13:15, :], rsm[:, 13:15, :], 1.0, None, ALU.subtract)
            nxt()
            for t in range(TT):
                ts(sel[:, t, :], iota[:, 0:NSLOT], rsm[:, 13, t:t + 1], None, ALU.is_equal)
            nxt()
            for t in range(TT):
                i = stt(sel[:, t, :], iota[:, 0:NSLOT], rsm[:, 14, t:t + 1], sel[:, t, :], ALU.is_equal, ALU.add)
            i.then_inc(sem("sel"), 1)
            dve.memset(xs[:, :, NSLOT:NSLOT + WIN], 0.0)
            for k in range(0, KT, 2):
                dve.wait_ge(*event("gather_mm", k + 1))
                if k:
                    dve.wait_ge(*event("gathered", k))
                ts(xs[:, k, 0:NSLOT], bank[2 + k % 4][:], ngf[:, k:k + 1], None, ALU.mult).then_inc(sem("gathered"), 1)
            dve.wait_ge(*event("gathered", KT))
            dve.memset(swT, 0.0)
            dve.memset(ysb, 0.0)
            dve.drain().then_inc(sem("y"), 1)
            dve.engine_nop().then_inc(sem("hidden"), 1)
            dve.engine_nop().then_inc(sem("x2"), 1)

            def add(v, t):
                dve.wait_ge(*event("c_mm", 2 * v - 1 + t))
                for j in range(4):
                    o = x_tok[:, t, j * 512:j * 512 + 512]
                    i = tt(o, o, bank[4 + j][:], ALU.add)
                i.then_inc(sem("x2"), 1)

            def window(v, c):
                dve.tensor_copy(xw, xs[:, :, ds(c, WIN)]).then_inc(sem("xw"), 1)
                add(v, 0)
                dve.wait_ge(*event("gate_sig", v))
                tt(eg, eg, bank[0][:, 0:P], ALU.mult)
                for t in range(TT):
                    i = ts(sw[:, t, :].rearrange("p (j s) -> p j s", j=4), bc(iota[:, ds(c, WIN)].unsqueeze(1), [P, 4, WIN]),
                           pw[:, t:t + 1], pw[:, 2 + t:3 + t], ALU.is_equal, ALU.mult)
                i.then_inc(sem("sw"), 1)
                nxt()
                dve.wait_ge(*event("up_mm", v))
                tt(hh, eg, bank[1][:, 0:P], ALU.mult).then_inc(sem("hidden"), 1)
                add(v, 1)

            with dve.Fori(0, NE) as e:
                more = dve.value_load(jobs[0:1, 0, ds(e, 1)], min_val=0, max_val=7)
                w0 = dve.value_load(jobs[0:1, 1, ds(e, 1)], min_val=0, max_val=64)
                c0 = dve.value_load(jobs[0:1, 2, ds(e, 1)], min_val=0, max_val=NSLOT)
                dve.tensor_copy(pw[:], posw[:, :, ds(e, 1)].rearrange("p a e -> p (a e)"))
                nxt()
                with dve.Fori(0, more + 1) as w:
                    c = nc.s_assert_within(c0 + w * WIN, 0, NSLOT, skip_runtime_bounds_check_because=
                                           "a window starts before its expert's last slot")
                    window(w0 + w + 1, c)
            more = dve.value_load(jobs[0:1, 0, NE - 1:NE], min_val=0, max_val=7)
            w0 = dve.value_load(jobs[0:1, 1, NE - 1:NE], min_val=0, max_val=64)
            for t in range(TT):
                add(w0 + more + 2, t)
            dve.drain().then_inc(sem("x2_all"), 1)

            dve.wait_ge(*event("pT_mm", 1))
            dve.tensor_copy(kT_sw[:].rearrange("p j s -> p (j s)"), bank[0][:]).then_inc(sem("pT"), 1)

            def projected(i):
                n, t = i // 2, i % 2
                dve.wait_ge(*event("pple_mm", i + 1))
                dve.tensor_copy(pple[:, t, n * 512:n * 512 + 512], bank[i % 4][:]).then_inc(sem("pple"), 1)

            for i in range(3):
                projected(i)
            dve.wait_ge(*event("x3_rms", 1))
            for t in range(TT):
                ts(x3n[:, t, :], x_tok[:, t, :], rs2[:, 4 + t:5 + t], None, ALU.mult).then_inc(sem("x3n"), 1)
            for i in range(3, 8):
                projected(i)

            evac_T(x3T, "x3T", ngp)
            for i in range(8):
                n, t = i // 2, i % 2
                c = slice(n * 512, n * 512 + 512)
                dve.wait_ge(*event("ple_sig", i + 1))
                tt(pe_e[i % 2], pe_e[i % 2], pple[:, t, c], ALU.mult)
                nxt()
                tt(x_tok[:, t, c], x_tok[:, t, c], pe_e[i % 2], ALU.add).then_inc(sem("result"), 1)


_INS = ["x", "p", "mix_norm", "w_in", "swa_q_norm", "swa_k_norm", "swa_sinks", "sb_q_norm", "sb_k_norm", "dn_conv",
        "dn_a_log", "dn_dt_bias", "dn_out_norm", "w_branch_a", "w_branch_b", "w_branch_c", "w_out", "ffn_norm",
        "w_group", "b_group", "w_router", "b_router", "w_e_gate", "w_e_up", "w_e_down", "ple_norm", "w_ple_gate",
        "w_ple_proj"]


def kernel(**inputs):
    import numpy as _np
    import concourse.bacc as _bacc
    from concourse.bass_utils import run_bass_kernel_spmd as _run

    nc = _bacc.Bacc("TRN2", target_bir_lowering=False, num_devices=1)
    arrays, args = {}, []
    for name in _INS:
        a = _np.ascontiguousarray(inputs[name])
        arrays[f"in_{name}"] = a
        args.append(nc.dram_tensor(f"in_{name}", a.shape, mybir.dt.from_np(a.dtype), kind="ExternalInput").ap())
    args.append(nc.dram_tensor("out_0", (1, S, D), F32, kind="ExternalOutput").ap())
    hybrid_trunk(nc, *args)
    r = _run(nc, [arrays], core_ids=[0])
    return r.results[0]["out_0"]
```
